# Optimizing a Trainium2 kernel written in Bass

```python
import math
import jax
import jax.numpy as jnp
from jax import lax
import numpy as np

D_MODEL = 1024
BATCH = 1
SEQ = 256
DEPTH = 2

CTX_LEN = 256
GRID_W = 64
N_EVEN = (DEPTH + 1) // 2
N_ODD = DEPTH // 2
N_MOD = 6
NORM_EPS = 1e-6

D_LRU = D_MODEL // 2
LRU_HEADS = 8
LRU_HEAD_DIM = D_LRU // LRU_HEADS
LRU_CONV_W = 4
LRU_C = 8.0
D_CONV = D_MODEL // 2
CONF_WIDTH = 31
EVEN_IN = 2 * D_LRU + 2 * D_CONV
EVEN_OUT = D_LRU + D_CONV
HEAD_DIM = 128
N_Q_HEADS = D_MODEL // HEAD_DIM
N_KV_HEADS = 2
GQA_GROUP = N_Q_HEADS // N_KV_HEADS
ROT_AXIS_DIM = HEAD_DIM // 2
ROPE_THETA = 10000.0
Q_BLOCK = 128
ODD_IN = (N_Q_HEADS + 2 * N_KV_HEADS) * HEAD_DIM
N_EXPERTS = 16
N_GROUPS = 4
EXPERTS_PER_GROUP = N_EXPERTS // N_GROUPS
TOP_K = 2
D_EXPERT = D_MODEL // 2

kernel_name = 'hybrid_rglru_conformer_gqa_moe_dit'

def rmsnorm(x, g):
    xf = x.astype(jnp.float32)
    y = xf * lax.rsqrt(jnp.mean(xf * xf, axis=-1, keepdims=True) + NORM_EPS)
    return (y * g.astype(jnp.float32)).astype(x.dtype)

def layernorm(x, g, b):
    xf = x.astype(jnp.float32)
    xc = xf - jnp.mean(xf, axis=-1, keepdims=True)
    var = jnp.mean(xc * xc, axis=-1, keepdims=True)
    y = xc * lax.rsqrt(var + NORM_EPS) * g.astype(jnp.float32) + b.astype(jnp.float32)
    return y.astype(x.dtype)

def modulate(h, shift, scale):
    return h * (1.0 + scale) + shift

def depthwise_conv(x, w, b, pad_left):
    k = w.shape[0]
    y = lax.conv_general_dilated(
        x, w[:, None, :].astype(x.dtype), window_strides=(1,),
        padding=[(pad_left, k - 1 - pad_left)],
        dimension_numbers=('NWC', 'WIO', 'NWC'),
        feature_group_count=x.shape[-1])
    return y + b

def _affine_compose(earlier, later):
    a1, b1 = earlier
    a2, b2 = later
    return a1 * a2, a2 * b1 + b2

def linear_scan(a, b, h0, reverse):
    a_cum, b_cum = lax.associative_scan(_affine_compose, (a, b), axis=1, reverse=reverse)
    return b_cum + a_cum * h0[:, None, :]

def rglru_coefficients(u, w_r, b_r, w_i, b_i, lam):
    bsz, t, _ = u.shape
    uh = u.reshape(bsz, t, LRU_HEADS, LRU_HEAD_DIM)
    r = jax.nn.sigmoid(jnp.einsum('bthi,hij->bthj', uh, w_r) + b_r).reshape(bsz, t, D_LRU)
    i = jax.nn.sigmoid(jnp.einsum('bthi,hij->bthj', uh, w_i) + b_i).reshape(bsz, t, D_LRU)
    log_a = -LRU_C * r * jax.nn.softplus(-lam)
    a = jnp.exp(log_a)
    b = jnp.sqrt(-jnp.expm1(2.0 * log_a)) * (i * u)
    return a, b

def rglru_group(x_c, x_l, conv_w, conv_b, w_r, b_r, w_i, b_i, lam):
    u_c = depthwise_conv(x_c, conv_w, conv_b, LRU_CONV_W // 2).astype(jnp.float32)
    u_l = depthwise_conv(x_l, conv_w, conv_b, LRU_CONV_W // 2).astype(jnp.float32)
    h0 = jnp.zeros((x_c.shape[0], D_LRU), jnp.float32)
    y_c = jnp.zeros_like(u_c)
    y_l = jnp.zeros_like(u_l)
    for d, reverse in enumerate((False, True)):
        a_c, b_c = rglru_coefficients(u_c, w_r[d], b_r[d], w_i[d], b_i[d], lam[d])
        h_c = linear_scan(a_c, b_c, h0, reverse)
        h_ctx_final = h_c[:, 0] if reverse else h_c[:, -1]
        a_l, b_l = rglru_coefficients(u_l, w_r[d], b_r[d], w_i[d], b_i[d], lam[d])
        h_l = linear_scan(a_l, b_l, h_ctx_final, reverse)
        y_c = y_c + h_c
        y_l = y_l + h_l
    return y_c, y_l

def conformer_conv_group(u, dw_w, dw_b, ln_g, ln_b):
    val, gate = jnp.split(u, 2, axis=-1)
    v = val * jax.nn.sigmoid(gate)
    v = depthwise_conv(v, dw_w, dw_b, CONF_WIDTH // 2)
    return jax.nn.silu(layernorm(v, ln_g, ln_b))

def recurrent_conv_mixer(h_c, h_l, w_in, w_out, conv_w, conv_b, w_r, b_r, w_i, b_i, lam,
                         dw_w, dw_b, ln_g, ln_b, need_ctx):
    splits = (D_LRU, 2 * D_LRU)
    xa_c, ga_c, ub_c = jnp.split(h_c @ w_in, splits, axis=-1)
    xa_l, ga_l, ub_l = jnp.split(h_l @ w_in, splits, axis=-1)
    s_c, s_l = rglru_group(xa_c, xa_l, conv_w, conv_b, w_r, b_r, w_i, b_i, lam)
    ya_l = s_l.astype(h_l.dtype) * jax.nn.gelu(ga_l)
    yb_l = conformer_conv_group(ub_l, dw_w, dw_b, ln_g, ln_b)
    out_l = jnp.concatenate([ya_l, yb_l], axis=-1) @ w_out
    if not need_ctx:
        return None, out_l
    ya_c = s_c.astype(h_c.dtype) * jax.nn.gelu(ga_c)
    yb_c = conformer_conv_group(ub_c, dw_w, dw_b, ln_g, ln_b)
    out_c = jnp.concatenate([ya_c, yb_c], axis=-1) @ w_out
    return out_c, out_l

def axial_rope_tables(rows):
    r, col = jnp.meshgrid(jnp.arange(rows, dtype=jnp.float32), jnp.arange(GRID_W, dtype=jnp.float32), indexing='ij')
    inv_freq = ROPE_THETA ** (-jnp.arange(0, ROT_AXIS_DIM, 2, dtype=jnp.float32) / ROT_AXIS_DIM)
    ang_r = r.reshape(-1)[:, None] * inv_freq
    ang_c = col.reshape(-1)[:, None] * inv_freq
    return jnp.cos(ang_r), jnp.sin(ang_r), jnp.cos(ang_c), jnp.sin(ang_c)

def rope_axis(x, cos, sin):
    x1, x2 = jnp.split(x, 2, axis=-1)
    cos = cos[None, :, None, :]
    sin = sin[None, :, None, :]
    return jnp.concatenate([x1 * cos - x2 * sin, x2 * cos + x1 * sin], axis=-1)

def axial_rope(x, rope):
    cos_r, sin_r, cos_c, sin_c = rope
    x_row, x_col = jnp.split(x.astype(jnp.float32), 2, axis=-1)
    y = jnp.concatenate([rope_axis(x_row, cos_r, sin_r), rope_axis(x_col, cos_c, sin_c)], axis=-1)
    return y.astype(x.dtype)

def gqa_attend(q, k, v):
    s = jnp.einsum('bqhgd,bshd->bhgqs', q, k).astype(jnp.float32) * (1.0 / math.sqrt(HEAD_DIM))
    p = jax.nn.softmax(s, axis=-1).astype(v.dtype)
    return jnp.einsum('bhgqs,bshd->bqhgd', p, v)

def attention_mixer(h_c, h_l, w_qkv, w_out, q_g, k_g, rope, need_ctx):
    bsz, s_len, _ = h_l.shape
    c_len = h_c.shape[1]

    def project(h):
        t = h.shape[1]
        q, k, v = jnp.split(h @ w_qkv, (N_Q_HEADS * HEAD_DIM, (N_Q_HEADS + N_KV_HEADS) * HEAD_DIM), axis=-1)
        q = rmsnorm(q.reshape(bsz, t, N_Q_HEADS, HEAD_DIM), q_g)
        k = rmsnorm(k.reshape(bsz, t, N_KV_HEADS, HEAD_DIM), k_g)
        return q, k, v.reshape(bsz, t, N_KV_HEADS, HEAD_DIM)

    q_c, k_c, v_c = project(h_c)
    q_l, k_l, v_l = project(h_l)
    q_l = axial_rope(q_l, rope)
    k_l = axial_rope(k_l, rope)
    k_all = jnp.concatenate([k_c, k_l], axis=1)
    v_all = jnp.concatenate([v_c, v_l], axis=1)
    n_blocks = s_len // Q_BLOCK
    q_blocks = q_l.reshape(bsz, n_blocks, Q_BLOCK, N_KV_HEADS, GQA_GROUP, HEAD_DIM).transpose(1, 0, 2, 3, 4, 5)
    o_l = lax.map(lambda qb: gqa_attend(qb, k_all, v_all), q_blocks)
    o_l = o_l.transpose(1, 0, 2, 3, 4, 5).reshape(bsz, s_len, N_Q_HEADS * HEAD_DIM)
    out_l = o_l @ w_out
    if not need_ctx:
        return None, out_l
    o_c = gqa_attend(q_c.reshape(bsz, c_len, N_KV_HEADS, GQA_GROUP, HEAD_DIM), k_c, v_c)
    out_c = o_c.reshape(bsz, c_len, N_Q_HEADS * HEAD_DIM) @ w_out
    return out_c, out_l

def grouped_moe(h, router_w, router_bias, w_gate, w_up, w_down):
    scores = jax.nn.sigmoid((h @ router_w).astype(jnp.float32))
    sel = scores + router_bias.astype(jnp.float32)
    grp_score = lax.top_k(sel.reshape(-1, N_GROUPS, EXPERTS_PER_GROUP), 2)[0].sum(-1)
    best = jnp.argmax(grp_score, axis=-1)
    in_group = (jnp.arange(N_EXPERTS) // EXPERTS_PER_GROUP)[None, :] == best[:, None]
    _, idx = lax.top_k(jnp.where(in_group, sel, -jnp.inf), TOP_K)
    w = jnp.take_along_axis(scores, idx, axis=-1)
    w = w / jnp.sum(w, axis=-1, keepdims=True)
    gates = jnp.sum(jax.nn.one_hot(idx, N_EXPERTS, dtype=jnp.float32) * w[..., None], axis=1)
    out = jnp.zeros_like(h)
    for e in range(N_EXPERTS):
        y = (jax.nn.silu(h @ w_gate[e]) * (h @ w_up[e])) @ w_down[e]
        out = out + gates[:, e:e + 1].astype(h.dtype) * y
    return out

def setup_inputs(seed: int = 0) -> dict:
    key = jax.random.key(seed)
    ks = jax.random.split(key, 32)
    f32 = jnp.float32

    def nrm(k, shape, scale):
        return jax.random.normal(k, shape, f32) * scale

    a0 = jax.random.uniform(ks[14], (N_EVEN, 2, D_LRU), f32, 0.9, 0.999)
    return {
        'x': nrm(ks[0], (BATCH, SEQ, D_MODEL), 1.0),
        'c': nrm(ks[1], (BATCH, D_MODEL), 1.0),
        'ctx': nrm(ks[2], (BATCH, CTX_LEN, D_MODEL), 1.0),
        'c_ctx': nrm(ks[3], (D_MODEL,), 1.0),
        'ada_w': nrm(ks[4], (DEPTH, D_MODEL, N_MOD * D_MODEL), 0.5 * D_MODEL ** -0.5),
        'ada_b': nrm(ks[5], (DEPTH, N_MOD * D_MODEL), 0.02),
        'norm_mix_g': 1.0 + nrm(ks[6], (DEPTH, D_MODEL), 0.1),
        'norm_ffn_g': 1.0 + nrm(ks[7], (DEPTH, D_MODEL), 0.1),
        'ev_w_in': nrm(ks[8], (N_EVEN, D_MODEL, EVEN_IN), D_MODEL ** -0.5),
        'ev_w_out': nrm(ks[9], (N_EVEN, EVEN_OUT, D_MODEL), EVEN_OUT ** -0.5),
        'lru_conv_w': nrm(ks[10], (N_EVEN, LRU_CONV_W, D_LRU), LRU_CONV_W ** -0.5),
        'lru_conv_b': nrm(ks[11], (N_EVEN, D_LRU), 0.02),
        'lru_w_r': nrm(ks[12], (N_EVEN, 2, LRU_HEADS, LRU_HEAD_DIM, LRU_HEAD_DIM), LRU_HEAD_DIM ** -0.5),
        'lru_b_r': nrm(ks[13], (N_EVEN, 2, LRU_HEADS, LRU_HEAD_DIM), 0.1),
        'lru_w_i': nrm(ks[15], (N_EVEN, 2, LRU_HEADS, LRU_HEAD_DIM, LRU_HEAD_DIM), LRU_HEAD_DIM ** -0.5),
        'lru_b_i': nrm(ks[16], (N_EVEN, 2, LRU_HEADS, LRU_HEAD_DIM), 0.1),
        'lru_lambda': jnp.log(a0) - jnp.log1p(-a0),
        'cf_dw_w': nrm(ks[17], (N_EVEN, CONF_WIDTH, D_CONV), CONF_WIDTH ** -0.5),
        'cf_dw_b': nrm(ks[18], (N_EVEN, D_CONV), 0.02),
        'cf_ln_g': 1.0 + nrm(ks[19], (N_EVEN, D_CONV), 0.1),
        'cf_ln_b': nrm(ks[20], (N_EVEN, D_CONV), 0.02),
        'at_w_qkv': nrm(ks[21], (N_ODD, D_MODEL, ODD_IN), D_MODEL ** -0.5),
        'at_w_out': nrm(ks[22], (N_ODD, N_Q_HEADS * HEAD_DIM, D_MODEL), (N_Q_HEADS * HEAD_DIM) ** -0.5),
        'at_q_norm_g': 1.0 + nrm(ks[23], (N_ODD, HEAD_DIM), 0.1),
        'at_k_norm_g': 1.0 + nrm(ks[24], (N_ODD, HEAD_DIM), 0.1),
        'router_w': nrm(ks[25], (D_MODEL, N_EXPERTS), D_MODEL ** -0.5),
        'router_bias': nrm(ks[26], (N_EXPERTS,), 0.01),
        'exp_w_gate': nrm(ks[27], (DEPTH, N_EXPERTS, D_MODEL, D_EXPERT), D_MODEL ** -0.5),
        'exp_w_up': nrm(ks[28], (DEPTH, N_EXPERTS, D_MODEL, D_EXPERT), D_MODEL ** -0.5),
        'exp_w_down': nrm(ks[29], (DEPTH, N_EXPERTS, D_EXPERT, D_MODEL), D_EXPERT ** -0.5),
        'final_norm_g': 1.0 + nrm(ks[30], (D_MODEL,), 0.1),
    }

def reference(x, c, ctx, c_ctx, ada_w, ada_b, norm_mix_g, norm_ffn_g, ev_w_in, ev_w_out,
              lru_conv_w, lru_conv_b, lru_w_r, lru_b_r, lru_w_i, lru_b_i, lru_lambda,
              cf_dw_w, cf_dw_b, cf_ln_g, cf_ln_b, at_w_qkv, at_w_out, at_q_norm_g, at_k_norm_g,
              router_w, router_bias, exp_w_gate, exp_w_up, exp_w_down, final_norm_g):
    bsz, s_len, d = x.shape
    c_len = ctx.shape[1]
    ROWS = s_len // GRID_W
    rope = axial_rope_tables(ROWS)
    silu_c = jax.nn.silu(c)
    silu_cc = jax.nn.silu(c_ctx)
    x_l, x_c = x, ctx
    for l in range(DEPTH):
        need_ctx = l < DEPTH - 1
        mod_l = (silu_c @ ada_w[l] + ada_b[l]).reshape(bsz, 1, N_MOD, d)
        mod_c = (silu_cc @ ada_w[l] + ada_b[l]).reshape(1, 1, N_MOD, d)
        sh1_l, sc1_l, g1_l, sh2_l, sc2_l, g2_l = [mod_l[:, :, i] for i in range(N_MOD)]
        sh1_c, sc1_c, g1_c, sh2_c, sc2_c, g2_c = [mod_c[:, :, i] for i in range(N_MOD)]
        h_l = modulate(rmsnorm(x_l, norm_mix_g[l]), sh1_l, sc1_l)
        h_c = modulate(rmsnorm(x_c, norm_mix_g[l]), sh1_c, sc1_c)
        if l % 2 == 0:
            e = l // 2
            y_c, y_l = recurrent_conv_mixer(
                h_c, h_l, ev_w_in[e], ev_w_out[e], lru_conv_w[e], lru_conv_b[e],
                lru_w_r[e], lru_b_r[e], lru_w_i[e], lru_b_i[e], lru_lambda[e],
                cf_dw_w[e], cf_dw_b[e], cf_ln_g[e], cf_ln_b[e], need_ctx)
        else:
            o = l // 2
            y_c, y_l = attention_mixer(h_c, h_l, at_w_qkv[o], at_w_out[o], at_q_norm_g[o], at_k_norm_g[o],
                                       rope, need_ctx)
        x_l = x_l + g1_l * y_l
        h_l = modulate(rmsnorm(x_l, norm_ffn_g[l]), sh2_l, sc2_l)
        if need_ctx:
            x_c = x_c + g1_c * y_c
            h_c = modulate(rmsnorm(x_c, norm_ffn_g[l]), sh2_c, sc2_c)
            tokens = jnp.concatenate([h_c.reshape(-1, d), h_l.reshape(-1, d)], axis=0)
            f = grouped_moe(tokens, router_w, router_bias, exp_w_gate[l], exp_w_up[l], exp_w_down[l])
            x_c = x_c + g2_c * f[:bsz * c_len].reshape(bsz, c_len, d)
            x_l = x_l + g2_l * f[bsz * c_len:].reshape(bsz, s_len, d)
        else:
            f = grouped_moe(h_l.reshape(-1, d), router_w, router_bias, exp_w_gate[l], exp_w_up[l], exp_w_down[l])
            x_l = x_l + g2_l * f.reshape(bsz, s_len, d)
    return rmsnorm(x_l, final_norm_g)


_drawn_inputs = setup_inputs


def setup_inputs(seed=0):
    import zlib

    import numpy as np

    out = dict(_drawn_inputs(seed))
    spreads = {}
    factors = {'cf_ln_b': 3.872, 'at_q_norm_g': 6.547, 'at_k_norm_g': 6.052}
    for name, (base, spread) in spreads.items():
        noise = np.random.default_rng([zlib.crc32(name.encode()), seed]).standard_normal(out[name].shape)
        drawn = base * np.exp(spread * noise) if base else spread * noise
        out[name] = jnp.asarray(drawn.astype(out[name].dtype))
    for name, factor in factors.items():
        out[name] = (out[name] * factor).astype(out[name].dtype)
    return out
```

```python
from contextlib import ExitStack

import numpy as np

import concourse.bass as bass
from concourse import mybir

F32 = mybir.dt.float32
BF16 = mybir.dt.bfloat16
I32 = mybir.dt.int32
ALU = mybir.AluOpType
ACT = mybir.ActivationFunctionType
AX = mybir.AxisListType.X

P = 128
D = 1024
KD = D // P
CTX, SEQ = 256, 256
TOK = CTX + SEQ
NT = TOK // P
CT = CTX // P
NMOD = 6
EPS = 1e-6
CH = 512
RING = 6
DL = D // 2
JT = DL // P
TAPS_L, LEFT_L = 4, 2
TAPS_C, LEFT_C = 31, 15
LRU_C = 8.0
HEADS, KVH, DH = 8, 2, 128
GROUP = HEADS // KVH
E, EG = 16, 4
FE = D // 2
MT = 64
GMAX = 34
MAXT = TOK // MT

C_C, C_CC, C_MIXG, C_CONVB, C_CONVW = 0, 8, 16, 32, 36
C_BR, C_BI, C_LAM, C_DWB, C_LNG, C_LNB, C_FFNG = 52, 60, 68, 76, 80, 84, 88
N_A = 104
C_DWW, N_B = 104, TAPS_C * JT
C_ADAB, N_C = 104 + TAPS_C * JT, 96
SH1, SC1, G1, SH2, SC2, G2 = range(NMOD)
LAT, CON = 0, 1

PRE = [("ada", 0, c) for c in range(4)]
_rest = [("ada", 0, c) for c in range(4, 12)] + [("ada", 1, c) for c in range(12)]
for _n, _c in enumerate((3, 2, 0, 1)):
    PRE += [("in", 0, _c)] + _rest[4 * _n:4 * _n + 4]
PRE += _rest[16:] + [("out0", 0, 0), ("out0", 0, 1)]
MID = [("qkv", 0, 2), ("qkv", 0, 0), ("qkv", 0, 1), ("out1", 0, 0), ("out1", 0, 1)]
PAIRS = E // 2


def build(nc, a):
    assert len(PRE) % RING == 0 and 2 * 3 == RING
    ahead = [[len(PRE) // RING] * RING, [len(PRE) // RING + PAIRS + (i < len(MID)) for i in range(RING)]]
    with ExitStack() as ctx:
        def sb(name, shape, dt=F32):
            return ctx.enter_context(nc.sbuf_tensor(name, shape, dt))

        def sem(name):
            return ctx.enter_context(nc.semaphore(name))

        h_dram = [nc.dram_tensor(f"h_rows{l}", [(TOK, SEQ)[l], D], F32, kind="Internal").ap() for l in range(2)]
        y_dram = nc.dram_tensor("y_rows", [32 * MT, D], F32, kind="Internal").ap()

        ps = ctx.enter_context(nc.psum_tensor("ps", [P, 8, 512], F32))

        ring = sb("weight_ring", [P, RING, 4096])
        x = sb("x", [P, NT, D])
        hT = sb("hT", [P, KD, TOK])
        arena = sb("arena", [P, 15648])
        ident = sb("ident", [P, P])
        ones512 = sb("ones512", [P, P])
        sel = sb("sel", [P, E])
        onesb = sb("onesb", [P, P], BF16)
        trib = sb("trib", [P, P], BF16)
        iota_s = sb("iota_s", [P, P])
        iota_g = sb("iota_g", [P, GMAX])
        thr = sb("thr", [P, MAXT - 1])
        tile_no = sb("tile_no", [P, 2, NT])
        tie = sb("tie", [P, 4, 4])
        pcol = sb("pcol", [P, 4])
        epsc = sb("epsc", [P, 1])
        ones16 = sb("ones16", [P, E])
        par = sb("par", [P, N_A + N_B + N_C])
        cond = sb("cond", [P, KD, 32])
        ada_part = sb("ada_part", [P, 2, 512])
        mods = sb("mods", [P, 2, NMOD * KD, 2])
        a1 = sb("a1", [P, 2, KD, 2])
        a2 = sb("a2", [P, 2, KD, 2])
        wbd = sb("wbd", [P, 2, 2, JT, 64])
        hb = sb("hb", [P, 2, 8])
        kdec = sb("kdec", [P, 8])
        lam_t = sb("lam_t", [P, 4, 8])
        rw = sb("rw", [P, KD, 32])
        rbias = sb("rbias", [P, E])
        qg = sb("qg", [P, DH])
        kg = sb("kg", [P, DH])
        trig = sb("trig", [P, 2, 2, 2, 32])
        ss = sb("ss", [P, 4, NT])
        rstd = sb("rstd", [P, 4, NT])
        gates2 = sb("gates2", [P, 2, NT])
        row_i = sb("row_i", [P, 2, NT], I32)
        gidx = sb("gidx", [P, GMAX], I32)
        gcur = sb("gcur", [P, 1], I32)
        ctl = sb("ctl", [P, 3, E], I32)
        att = sb("att", [P, 4, 16])
        qk_ss = sb("qk_ss", [P, 2, 24])

        def reg(off, n):
            return arena[:, off:off + n]

        xn = reg(0, 4096).rearrange("p (t d) -> p t d", t=NT)
        sg = reg(0, 2048).rearrange("p (j n) -> p j n", j=JT)
        lru_sq, lru_hf, ln_r = reg(0, 512), reg(512, 512), reg(1024, 512)
        u = reg(2048, 2048).rearrange("p (j n) -> p j n", j=JT)
        VP, XP = CTX + TAPS_C - 1, CTX + TAPS_L - 1
        vpad = reg(4096, JT * 2 * VP).rearrange("p (j s n) -> p j s n", j=JT, s=2)
        xpad = reg(6400, JT * 2 * XP).rearrange("p (j s n) -> p j s n", j=JT, s=2)
        cat = reg(8480, 4096).rearrange("p (k n) -> p k n", k=KD)
        lru = [reg(12576, 3072).rearrange("p (b w n) -> p b w n", b=2, w=3),
               hT[:, 0:6, :].rearrange("p (b w) n -> p b w n", b=2)]
        conv_tap = reg(1536, 512)
        prow = reg(8480, 3 * P).rearrange("p (i n) -> p i n", i=3)
        mb = [reg(12576, D), reg(13600, D), reg(4096, D), reg(5120, D)]
        junk = reg(14624, 1024)
        hrow = reg(0, 4096).rearrange("p (t d) -> p t d", t=NT)
        q = reg(4096, 2048).rearrange("p (t n) -> p t n", t=2)
        kv = reg(6144, 2048).rearrange("p (t n) -> p t n", t=NT)
        qT = reg(8192, 2048).rearrange("p (h n) -> p h n", h=HEADS)
        kT = reg(10240, 1024).rearrange("p (h n) -> p h n", h=KVH)
        prob = reg(11264, 1024).rearrange("p (b n) -> p b n", b=2)
        pT = reg(0, 2048).rearrange("p (b k n) -> p b k n", b=2, k=NT)
        oT = reg(2048, 2048).rearrange("p (h n) -> p h n", h=HEADS)
        rope_t = reg(12576, 2048).rearrange("p (w n) -> p w n", w=4)
        sq_big = reg(0, 3072)
        xg, xgT = reg(0, 512), reg(512, 512).rearrange("p (k n) -> p k n", k=4)
        act_in, act_sl = reg(1024, 256), reg(1280, 256)
        actT = reg(1536, 256).rearrange("p (c n) -> p c n", c=2)
        y_sb = reg(2048, 512)
        yg = reg(4096, 8192).rearrange("p (c t d) -> p c t d", c=2, t=NT)
        fin = reg(0, 2048).rearrange("p (t d) -> p t d", t=2)
        fing = reg(2048, D)

        landed = [sem(f"chunk_landed{i}") for i in range(RING)]
        used = [sem(f"chunk_used{i}") for i in range(RING)]
        s_par, s_x, s_aux, s_fg = sem("param_rows_in"), sem("x_in"), sem("aux_in"), sem("final_gain_in")
        s_const, s_zero = sem("constants_made"), sem("pads_zeroed")
        s_parT, s_pc, s_cond = sem("param_transposed"), sem("param_table"), sem("cond_ready")
        s_ada, s_part, s_col = sem("ada_product"), sem("ada_partials"), sem("ada_columns")
        s_mods, s_a12 = sem("mods_ready"), sem("gains_ready")
        s_ss = [sem(f"squares{i}") for i in range(5)]
        s_xn = [sem(f"xn_ready{i}") for i in range(2)]
        s_xT = [sem(f"xn_transposed{i}") for i in range(2)]
        s_hTd = [sem(f"hT_even{i}") for i in range(2)]
        s_hTa = [sem(f"hT_odd{i}") for i in range(2)]
        s_in, s_sg, s_v, s_xa, s_ga = sem("in_product"), sem("glu_gate"), sem("glu_value"), sem("lru_in"), sem("gelu_gate")
        s_u, s_gm, s_gr, s_co, s_lru = sem("lru_conv"), sem("gate_product"), sem("gates_read"), sem("coeffs"), sem("lru_done")
        s_kd = sem("decay_exp")
        s_cvd, s_cvp = sem("conv_vector"), sem("conv_pool")
        s_mean, s_xc, s_sqc, s_var, s_nrm, s_cat = (sem("ln_mean"), sem("ln_centred"), sem("ln_squares"), sem("ln_var"),
                                                    sem("ln_scaled"), sem("mix_ready"))
        s_bcm, s_bc = sem("broadcast_product"), sem("broadcast_ready")
        s_op = [sem(f"out_product{l}") for l in range(2)]
        s_res = [sem(f"residual_added{l}") for l in range(2)]
        s_h = [sem(f"h_rows_ready{l}") for l in range(2)]
        s_hst = [sem(f"h_rows_stored{l}") for l in range(2)]
        s_h2m = [sem(f"h_transposed{l}") for l in range(2)]
        s_h2 = [sem(f"h_columns{l}") for l in range(2)]
        s_rp = [sem(f"router_product{l}") for l in range(2)]
        s_rpe = [sem(f"router_partials{l}") for l in range(2)]
        s_lg = [sem(f"logits{l}") for l in range(2)]
        s_sc = [sem(f"scores{l}") for l in range(2)]
        s_mask = [sem(f"expert_mask{l}") for l in range(2)]
        s_pos = [sem(f"positions{l}") for l in range(2)]
        s_oh = [sem(f"one_hots{l}") for l in range(2)]
        s_id = [sem(f"ids{l}") for l in range(2)]
        s_rt = [sem(f"routed{l}") for l in range(2)]
        s_gc = [sem(f"gather_index{l}") for l in range(2)]
        s_xg = [sem(f"tile_rows_in{l}") for l in range(2)]
        s_xt = [sem(f"tile_transposed{l}") for l in range(2)]
        s_xgT = [sem(f"tile_columns{l}") for l in range(2)]
        s_gu = [sem(f"gate_up_product{l}") for l in range(2)]
        s_sl = [sem(f"silu_done{l}") for l in range(2)]
        s_ac = [sem(f"expert_act{l}") for l in range(2)]
        s_at = [sem(f"act_transposed{l}") for l in range(2)]
        s_aT = [sem(f"act_columns{l}") for l in range(2)]
        s_dn = [sem(f"down_product{l}") for l in range(2)]
        s_y = [sem(f"tile_out{l}") for l in range(2)]
        s_yo = [sem(f"tile_out_stored{l}") for l in range(2)]
        s_yall = [sem(f"all_tiles_stored{l}") for l in range(2)]
        s_yg = [[sem(f"expert_rows_in{l}_{t}") for t in range(NT)] for l in range(2)]
        s_x2 = [sem(f"moe_added{l}") for l in range(2)]
        s_qkv, s_qkve, s_sq, s_qn = sem("qkv_product"), sem("qkv_read"), sem("qk_squares"), sem("qk_roped")
        s_qss = sem("qk_sums")
        s_qkT, s_qkTe = sem("qk_transposed"), sem("qk_columns")
        s_s, s_m, s_p, s_pn = sem("score_product"), sem("score_max"), sem("prob_exp"), sem("prob_scaled")
        s_pt, s_pte, s_o, s_oe = sem("prob_transposed"), sem("prob_columns"), sem("pv_product"), sem("pv_read")
        s_fill = sem("unused_rows_filled")
        s_gcd = sem("index_copied")
        s_fin, s_out = sem("final_rows"), sem("final_stored")
        s_rms = sem("rms_ready")
        s_sq1, s_sqr = sem("one_minus_square"), sem("square_root")
        s_dve, s_pool, s_act = sem("vector_step"), sem("pool_step"), sem("scalar_step")

        def chunk_src(kind, l, c):
            if kind == "ada":
                w = a["ada_w"][l]
            elif kind == "in":
                w = a["ev_w_in"][0]
            elif kind == "out0":
                w = a["ev_w_out"][0]
            elif kind == "qkv":
                w = a["at_w_qkv"][0]
            else:
                w = a["at_w_out"][0]
            return w.rearrange("(k p) n -> p k n", p=P)[:, :, CH * c:CH * c + CH]

        def wide(slot):
            return ring[:, slot, :].rearrange("p (k n) -> p k n", k=KD)

        def deep(slot):
            return ring[:, slot, :].rearrange("p (k n) -> p k n", k=4)

        def toks(l):
            return list(range(NT)) if l == 0 else list(range(CT, NT))

        def cond_of(t):
            return CON if t < CT else LAT

        def col_of(table, l, i):
            return {"m": mods[:, l, 8 * i:8 * i + 8, :] if i is not None else None, "a2": a2[:, l, :, :]}[table]

        BC = [("m", 0, G1, CON, 0), ("m", 0, G1, LAT, 1),
              ("a2", 0, None, CON, 2), ("m", 0, SH2, CON, 3), ("a2", 0, None, LAT, 0), ("m", 0, SH2, LAT, 1),
              ("m", 0, G2, CON, 0), ("m", 0, G2, LAT, 1),
              ("m", 1, G1, LAT, 0), ("a2", 1, None, LAT, 2), ("m", 1, SH2, LAT, 3), ("m", 1, G2, LAT, 0)]

        RT = 4096 + 2048

        def rt(off, n):
            return reg(RT + off, n)

        def mask_b(l):
            n = len(toks(l))
            return rt(0, 32).bitcast(BF16)[:, 0:16 * n].rearrange("p (t e) -> p t e", t=n)

        def oh_slot(l):
            n = len(toks(l))
            return rt(64, 512).bitcast(BF16)[:, 0:2 * n * P].rearrange("p (i s) -> p i s", s=P)

        def oh_tile(l):
            n = len(toks(l))
            return rt(576, 272).bitcast(BF16)[:, 0:2 * n * 2 * GMAX].rearrange("p (i w g) -> p i w g", w=2, g=GMAX)

        def score_sb(l):
            return rt(960, 64)[:, 0:E * len(toks(l))]

        block = ctx.enter_context(nc.Block())

        @block.sync
        def _(sp):
            rows = [("c", C_C, 8, a["c"].rearrange("b (k n) -> (b k) n", n=P)),
                    ("cc", C_CC, 8, a["c_ctx"].rearrange("(k n) -> k n", n=P)),
                    ("mixg", C_MIXG, 16, a["norm_mix_g"].rearrange("l (k n) -> (l k) n", n=P)),
                    ("convb", C_CONVB, 4, a["lru_conv_b"].rearrange("e (k n) -> (e k) n", n=P)),
                    ("convw", C_CONVW, 16, a["lru_conv_w"].rearrange("e w (k n) -> (e w k) n", n=P)),
                    ("br", C_BR, 8, a["lru_b_r"].rearrange("e d (k h) n -> (e d k) (h n)", h=2)),
                    ("bi", C_BI, 8, a["lru_b_i"].rearrange("e d (k h) n -> (e d k) (h n)", h=2)),
                    ("lam", C_LAM, 8, a["lru_lambda"].rearrange("e d (k n) -> (e d k) n", n=P)),
                    ("dwb", C_DWB, 4, a["cf_dw_b"].rearrange("e (k n) -> (e k) n", n=P)),
                    ("lng", C_LNG, 4, a["cf_ln_g"].rearrange("e (k n) -> (e k) n", n=P)),
                    ("lnb", C_LNB, 4, a["cf_ln_b"].rearrange("e (k n) -> (e k) n", n=P)),
                    ("ffng", C_FFNG, 16, a["norm_ffn_g"].rearrange("l (k n) -> (l k) n", n=P))]
            for _, at, n, src in rows:
                sp.dma_start(prow[at:at + n, 0, :], src).then_inc(s_par, 16)
            sp.dma_start(prow[0:N_B, 1, :], a["cf_dw_w"].rearrange("e w (k n) -> (e w k) n", n=P)).then_inc(s_par, 16)
            sp.dma_start(prow[0:N_C, 2, :], a["ada_b"].rearrange("l (k n) -> (l k) n", n=P)).then_inc(s_par, 16)

            for i, (kind, l, c) in enumerate(PRE):
                if i >= RING:
                    sp.wait_ge(used[i % RING], i // RING)
                sp.dma_start(wide(i % RING), chunk_src(kind, l, c)).then_inc(landed[i % RING], 16)

            def experts(l):
                mats = [a["exp_w_gate"][l], a["exp_w_up"][l], a["exp_w_down"][l]]
                with sp.Fori(0, PAIRS) as pair:
                    for b in range(2):
                        for m in range(3):
                            slot = 3 * b + m
                            w = mats[m].rearrange("(pr b) (k p) n -> pr b p k n", b=2, p=P)
                            dst = deep(slot) if m == 2 else wide(slot)
                            sp.wait_ge(used[slot], pair + ahead[l][slot])
                            sp.dma_start(dst, w[pair, b]).then_inc(landed[slot], 16)

            experts(0)
            for i, (kind, l, c) in enumerate(MID):
                sp.wait_ge(used[i], ahead[0][i] + PAIRS)
                sp.dma_start(wide(i), chunk_src(kind, l, c)).then_inc(landed[i], 16)
            experts(1)
            sp.wait_ge(s_fin, 2)
            sp.dma_start(a["out"].rearrange("b (t p) d -> p (b t) d", p=P), fin).then_inc(s_out, 16)
            sp.wait_ge(s_out, 16)

        @block.tensor
        def _(pe):
            mm = nc.tensor.matmul
            tr = nc.tensor.transpose
            pe.wait_ge(s_const, 1)
            pe.wait_ge(s_par, 16 * 14)
            tr(ps[:, 0, 0:N_A], prow[0:N_A, 0, :], ident[0:N_A, 0:N_A])
            tr(ps[:, 0, 128:128 + N_B], prow[0:N_B, 1, :], ident[0:N_B, 0:N_B])
            tr(ps[:, 0, 256:256 + N_C], prow[0:N_C, 2, :], ident[0:N_C, 0:N_C]).then_inc(s_parT, 1)

            seen = [0] * RING
            state = {"chunk": 0, "ada": 0}

            def next_chunk():
                slot = state["chunk"] % RING
                state["chunk"] += 1
                seen[slot] += 1
                pe.wait_ge(landed[slot], 16 * seen[slot])
                return slot

            def ada_product():
                n = state["ada"]
                slot = next_chunk()
                if n:
                    pe.wait_ge(s_part, n)
                else:
                    pe.wait_ge(s_cond, 1)
                for k in range(KD):
                    g = 32 * (k % 4)
                    last = mm(ps[g:g + 32, 6, :], cond[:, k, :], wide(slot)[:, k, :], start=(k < 4), stop=(k >= 4),
                              skip_group_check=True)
                last.then_inc(used[slot], 1)
                state["ada"] += 1

            def ada_signal():
                pe.wait_ge(used[(state["chunk"] - 1) % RING], seen[(state["chunk"] - 1) % RING])

            def ada_columns(n):
                pe.wait_ge(s_part, n + 1)
                for i in range(4):
                    last = mm(ps[:, 7, 8 * n + 2 * i:8 * n + 2 * i + 2], ada_part[:, n % 2, P * i:P * i + P],
                              sel[:, 0:2], start=True, stop=True)
                last.then_inc(s_col, 1)

            for n in range(4):
                ada_product()
                ada_columns(n)

            def xn_transposes(l):
                pe.wait_ge(s_xn[l], NT)
                for k in range(KD):
                    if k >= 4:
                        pe.wait_ge(s_hTd[l] if k % 2 == 0 else s_hTa[l], (k - 4) // 2 + 1)
                    for t in range(NT):
                        last = tr(ps[:, k % 4, P * t:P * t + P], xn[:, t, P * k:P * k + P], ident[:, :])
                    last.then_inc(s_xT[l], 1)
                pe.wait_ge(s_hTd[l], KD // 2)
                pe.wait_ge(s_hTa[l], KD // 2)

            xn_transposes(0)
            evac = [s_sg, s_v, s_xa, s_ga]
            for part in range(4):
                slot = next_chunk()
                for j in range(JT):
                    m = JT * part + j
                    if part:
                        pe.wait_ge(evac[part - 1], j + 1)
                    for k in range(KD):
                        last = mm(ps[:, j, :], wide(slot)[:, k, P * j:P * j + P], hT[:, k, :],
                                  start=(k == 0), stop=(k == KD - 1))
                    last.then_inc(s_in, 1)
                    if j == JT - 1:
                        pe.wait_ge(s_in, m + 1)
                        pe.sem_inc(used[slot], 1)
                    n = state["ada"]
                    if m:
                        ada_columns(n - 1)
                    ada_product()
            pe.wait_ge(s_aux, 16 * AUX)
            for qd in range(2 * JT):
                j, d = qd // 2, qd % 2
                pe.wait_ge(s_u, j + 1)
                if qd:
                    pe.wait_ge(s_gr, qd)
                for g in range(2):
                    for hf in (0, 64):
                        last = mm(ps[hf:hf + 64, 4 + g, :], wbd[hf:hf + 64, g, d, j, :], u[hf:hf + 64, j, :],
                                  start=True, stop=True)
                last.then_inc(s_gm, 1)
            for _ in range(4):
                ada_columns(state["ada"] - 1)
                ada_product()
            ada_columns(state["ada"] - 1)
            pe.wait_ge(s_gr, 2 * JT)
            pe.wait_ge(s_cvd, 1)
            pe.wait_ge(s_cvp, 1)
            for j in range(JT):
                last = mm(ps[:, 4, :], ones512[:, :], cat[:, JT + j, :], start=(j == 0), stop=(j == JT - 1))
            last.then_inc(s_mean, 1)
            for j in range(JT):
                pe.wait_ge(s_sqc, j + 1)
                last = mm(ps[:, 5, :], ones512[:, :], hT[:, j, :], start=(j == 0), stop=(j == JT - 1))
            last.then_inc(s_var, 1)

            def broadcast(n):
                table, l, i, v, _ = BC[n]
                col = col_of(table, l, i)
                if n:
                    pe.wait_ge(s_bc, n)
                for k in range(KD):
                    last = mm(ps[:, 6 + k // 4, P * (k % 4):P * (k % 4) + P],
                              col[:, k, v:v + 1].to_broadcast([P, P]), ident[:, :], start=True, stop=True)
                last.then_inc(s_bcm, 1)

            pe.wait_ge(s_mods, 2)
            pe.wait_ge(s_a12, 3)
            broadcast(0)
            broadcast(1)

            def project(l, tiles, lhs, ready):
                n_t = len(tiles)
                for c in range(2):
                    slot = next_chunk()
                    for i in range(n_t):
                        m = c * n_t + i
                        if m >= 4:
                            pe.wait_ge(s_res[l], m - 3)
                        for k in range(KD):
                            if m == 0:
                                ready(k)
                            last = mm(ps[:, m % 4, :], lhs(k, i), wide(slot)[:, k, :], start=(k == 0), stop=(k == KD - 1))
                        last.then_inc(s_op[l], 1)
                    pe.wait_ge(s_op[l], (c + 1) * n_t)
                    pe.sem_inc(used[slot], 1)

            def mix_ready(k):
                if k == 0:
                    pe.wait_ge(s_lru, JT)
                if k >= JT:
                    pe.wait_ge(s_cat, k - JT + 1)

            project(0, range(NT), lambda k, i: cat[:, k, P * i:P * i + P], mix_ready)

            def router(l):
                tiles = toks(l)
                n = len(tiles)
                for i, t in enumerate(tiles):
                    pe.wait_ge(s_h[l], i + 1)
                    pe.wait_ge(s_res[l], 2 * n)
                    if i >= 2:
                        pe.wait_ge(s_h2[l], i - 1)
                    for k in range(KD):
                        last = tr(ps[:, 2 * (i % 2) + k // 4, P * (k % 4):P * (k % 4) + P],
                                  hrow[:, t, P * k:P * k + P], ident[:, :])
                    last.then_inc(s_h2m[l], 1)
                pe.wait_ge(s_h2[l], n)
                w = n * P
                for k in range(KD):
                    g = 32 * (k % 4)
                    last = mm(ps[g:g + 32, 4, 0:w], rw[:, k, :], hT[:, k, TOK - w:TOK], start=(k < 4), stop=(k >= 4),
                              skip_group_check=True)
                last.then_inc(s_rp[l], 1)
                pe.wait_ge(s_rpe[l], 1)
                for i in range(n):
                    last = mm(ps[:, 5, E * i:E * i + E], ada_part[:, 0, P * i:P * i + P], sel[:, :], start=True, stop=True)
                last.then_inc(s_lg[l], 1)
                pe.wait_ge(s_mask[l], 1)
                mk = mask_b(l)
                mm(ps[:, 4, 0:E * n], trib[:, :], mk.rearrange("p t e -> p (t e)"), start=True, stop=(n == 1),
                   skip_group_check=True)
                for i in range(n - 1):
                    r = n - 1 - i
                    mm(ps[:, 4, E * (i + 1):E * n], onesb[:, :], mk[:, i:i + 1, :].to_broadcast([P, r, E]), start=False,
                       stop=(i == n - 2), skip_group_check=True)
                for i in range(n):
                    last = mm(ps[:, 5, 0:E], onesb[:, :], mk[:, i, :], start=(i == 0), stop=(i == n - 1))
                last.then_inc(s_pos[l], 1)
                pe.wait_ge(s_oh[l], 1)
                for i in range(2 * n):
                    last = mm(ps[:, 4, 0:2 * GMAX], oh_slot(l)[:, i, :], oh_tile(l)[:, i, :, :].rearrange("p w g -> p (w g)"),
                              start=(i == 0), stop=(i == 2 * n - 1))
                last.then_inc(s_id[l], 1)

            def tile_transposes(l, count):
                pe.wait_ge(s_xg[l], count * 16)
                for k in range(4):
                    last = tr(ps[:, 0, P * k:P * k + P], xg[:, P * k:P * k + P], ident[:, :])
                last.then_inc(s_xt[l], 1)

            def moe(l):
                pe.wait_ge(s_rt[l], 1)
                pe.sem_inc(s_xt[l], 1)
                tile_transposes(l, 1)
                with pe.Fori(0, PAIRS) as pair:
                    for b in range(2):
                        wg, wu, wd = wide(3 * b), wide(3 * b + 1), deep(3 * b + 2)
                        first = pe.value_load(ctl[0:1, 1, bass.ds(pair * 2 + b, 1)], min_val=0, max_val=31)
                        end = pe.value_load(ctl[0:1, 2, bass.ds(pair * 2 + b, 1)], min_val=1, max_val=32)

                        def weights(m):
                            pe.wait_ge(landed[3 * b + m], 16 * pair + 16 * (ahead[l][3 * b + m] + 1))

                        with pe.Fori(first, end) as g:
                            pe.wait_ge(s_xgT[l], g + 1)

                            def gate_up(c, w, bank):
                                for k in range(KD):
                                    for fh in range(2):
                                        last = mm(ps[64 * fh:64 * fh + 64, bank, P * c:P * c + P],
                                                  xgT[:, k % 4, 64 * (k // 4):64 * (k // 4) + 64],
                                                  w[:, k, 256 * fh + P * c:256 * fh + P * c + P],
                                                  start=(k == 0), stop=(k == KD - 1), skip_group_check=True)
                                return last

                            def act_transpose(c):
                                pe.wait_ge(s_ac[l], g * 2 + (c + 1))
                                tr(ps[:, 3, P * c:P * c + P], act_in[:, P * c:P * c + P], ident[:, :]).then_inc(s_at[l], 1)

                            def down(c):
                                pe.wait_ge(s_aT[l], g * 2 + (c + 1))
                                for fh in range(2):
                                    for n in range(2):
                                        last = mm(ps[64 * n:64 * n + 64, 4, :], actT[:, c, 64 * fh:64 * fh + 64],
                                                  wd[:, 2 * fh + c, 512 * n:512 * n + 512],
                                                  start=(c == 0 and fh == 0), stop=(c == 1 and fh == 1),
                                                  skip_group_check=True)
                                return last

                            weights(0)
                            gate_up(0, wg, GB[0])
                            weights(1)
                            gate_up(0, wu, UB[0]).then_inc(s_gu[l], 1)
                            gate_up(1, wg, GB[1])
                            act_transpose(0)
                            gate_up(1, wu, UB[1]).then_inc(s_gu[l], 1)
                            pe.wait_ge(s_y[l], g + 1)
                            weights(2)
                            down(0)
                            act_transpose(1)
                            tile_transposes(l, g + 2)
                            down(1).then_inc(s_dn[l], 1)
                        pe.wait_ge(s_dn[l], end + 0)
                        for m in range(3):
                            pe.sem_inc(used[3 * b + m], 1)
                for i in range(RING):
                    seen[i] += PAIRS

            for n in range(2, 6):
                broadcast(n)
            router(0)
            moe(0)
            broadcast(6)
            broadcast(7)

            xn_transposes(1)
            slot = next_chunk()
            for t in range(NT):
                for k in range(KD):
                    last = mm(ps[:, t, :], hT[:, k, P * t:P * t + P], wide(slot)[:, k, :], start=(k == 0), stop=(k == KD - 1))
                last.then_inc(s_qkv, 1)
            pe.wait_ge(s_qkv, NT)
            pe.sem_inc(used[slot], 1)
            pe.wait_ge(s_bc, 8)
            for c in range(2):
                slot = next_chunk()
                for i in range(2):
                    t = CT + i
                    for k in range(KD):
                        last = mm(ps[:, 4 + 2 * c + i, :], hT[:, k, P * t:P * t + P], wide(slot)[:, k, :],
                                  start=(k == 0), stop=(k == KD - 1))
                    last.then_inc(s_qkv, 1)
                pe.wait_ge(s_qkv, NT + 2 * c + 2)
                pe.sem_inc(used[slot], 1)
            pe.wait_ge(s_qkve, 8)
            pe.wait_ge(s_qn, 1)
            for kh in range(KVH):
                for t in range(NT):
                    last = tr(ps[:, kh, P * t:P * t + P], kv[:, t, DH * kh:DH * kh + DH], ident[:, :])
                last.then_inc(s_qkT, 1)
            pe.wait_ge(s_qn, 2)
            for g in range(4):
                for i in range(4):
                    h, t = 2 * g + i // 2, i % 2
                    last = tr(ps[:, 2 + g, P * i:P * i + P], q[:, t, DH * h:DH * h + DH], ident[:, :])
                last.then_inc(s_qkT, 1)
            pe.wait_ge(s_qkTe, 6)

            def scores(n):
                h, t = n // 2, n % 2
                if n >= 2:
                    pe.wait_ge(s_p, n - 1)
                mm(ps[:, n % 2, :], qT[:, h, P * t:P * t + P], kT[:, h // GROUP, :], start=True, stop=True).then_inc(s_s, 1)

            scores(0)
            scores(1)
            for n in range(2 * HEADS):
                h, t = n // 2, n % 2
                pe.wait_ge(s_pn, n + 1)
                if n >= 2:
                    pe.wait_ge(s_pte, n - 1)
                for k in range(NT):
                    last = tr(ps[:, 2 + n % 2, P * k:P * k + P], prob[:, n % 2, P * k:P * k + P], ident[:, :])
                last.then_inc(s_pt, 1)
                if n + 2 < 2 * HEADS:
                    scores(n + 2)
                if t == 1:
                    if h >= 2:
                        pe.wait_ge(s_oe, h - 1)
                    pe.wait_ge(s_pte, n + 1)
                    for k in range(NT):
                        last = mm(ps[:, 4 + h % 2, 0:SEQ], kv[:, k, KVH * DH + DH * (h // GROUP):KVH * DH + DH * (h // GROUP) + DH],
                                  pT[:, h % 2, k, :], start=(k == 0), stop=(k == NT - 1))
                    last.then_inc(s_o, 1)
            broadcast(8)

            def attended(k):
                if k == 0:
                    pe.wait_ge(s_oe, HEADS)

            project(1, range(2), lambda k, i: oT[:, k, P * i:P * i + P], attended)
            state["chunk"] += 1
            broadcast(9)
            broadcast(10)
            router(1)
            moe(1)
            broadcast(11)

        @block.vector
        def _(dve):
            v = nc.vector
            step = [0]

            def mark(ins):
                step[0] += 1
                ins.then_inc(s_dve, 1)
                return step[0]

            def link(ins):
                dve.wait_ge(s_dve, mark(ins))

            roots = [0]

            def invert(view):
                roots[0] += 1
                dve.wait_ge(s_rms, roots[0])
                link(v.reciprocal(view, view))

            dve.wait_ge(s_parT, 1)
            v.tensor_copy(par[:, 0:N_A], ps[:, 0, 0:N_A])
            v.tensor_copy(par[:, C_DWW:C_DWW + N_B], ps[:, 0, 128:128 + N_B])
            link(v.tensor_copy(par[:, C_ADAB:C_ADAB + N_C], ps[:, 0, 256:256 + N_C]))
            link(v.engine_nop())
            dve.sem_inc(s_pc, 1)

            def normalise(l, dst=None):
                invert(rstd[:, l, :])
                for t in range(NT):
                    v.tensor_scalar(xn[:, t, :], x[:, t, :], rstd[:, l, t:t + 1], None, ALU.mult).then_inc(s_xn[l], 1)

            def modulate_columns(l):
                for k in range(0, KD, 2):
                    dve.wait_ge(s_xT[l], k + 1)
                    for vv, lo in ((CON, 0), (LAT, CTX)):
                        last = v.tensor_scalar(hT[:, k, lo:lo + 256], ps[:, k % 4, lo:lo + 256], a1[:, l, k, vv:vv + 1],
                                               mods[:, l, 8 * SH1 + k, vv:vv + 1], ALU.mult, ALU.add)
                    last.then_inc(s_hTd[l], 1)

            dve.wait_ge(s_x, 32)
            normalise(0)
            dve.wait_ge(s_col, 4)

            def read_mods(l, n0, n1, c0):
                m = 4 * (n1 - n0)
                return v.tensor_tensor(mods[:, l, 4 * c0:4 * c0 + m, :],
                                       ps[:, 7, 8 * n0:8 * n1].rearrange("p (n v) -> p n v", v=2),
                                       par[:, C_ADAB + 48 * l + 4 * c0:C_ADAB + 48 * l + 4 * c0 + m].unsqueeze(2)
                                       .to_broadcast([P, m, 2]), ALU.add)

            link(read_mods(0, 0, 4, 0))

            def gain(dst, l, i, pcol0):
                return v.scalar_tensor_tensor(dst[:, l, :, :], mods[:, l, 8 * i:8 * i + 8, :], 1.0,
                                              par[:, pcol0:pcol0 + 8].unsqueeze(2).to_broadcast([P, 8, 2]), ALU.add, ALU.mult)

            link(gain(a1, 0, SC1, C_MIXG))
            dve.sem_inc(s_mods, 1)
            modulate_columns(0)
            link(v.tensor_scalar(hb[:, :, :].rearrange("p g n -> p (g n)"), par[:, C_BR:C_BR + 16], 0.5, None, ALU.mult))
            link(v.tensor_scalar(lam_t[:, 3, :], par[:, C_LAM:C_LAM + 8], -1.0, 0.0, ALU.mult, ALU.max))
            link(v.scalar_tensor_tensor(lam_t[:, 0, :], lam_t[:, 3, :], 2.0, par[:, C_LAM:C_LAM + 8], ALU.mult, ALU.add))
            dve.sem_inc(s_kd, 1)
            dve.wait_ge(s_act, 1)
            link(v.tensor_scalar(lam_t[:, 1, :], lam_t[:, 0, :], 1.0, None, ALU.add))
            dve.sem_inc(s_kd, 1)
            dve.wait_ge(s_act, 2)
            link(v.tensor_scalar(lam_t[:, 1, :], lam_t[:, 1, :], -1.0, None, ALU.add))
            link(v.tensor_scalar(kdec[:, :], lam_t[:, 1, :], 0.0, None, ALU.is_equal))
            link(v.tensor_tensor(lam_t[:, 1, :], lam_t[:, 1, :], kdec[:, :], ALU.add))
            link(v.tensor_tensor(lam_t[:, 2, :], lam_t[:, 2, :], kdec[:, :], ALU.add))
            link(v.reciprocal(lam_t[:, 1, :], lam_t[:, 1, :]))
            link(v.tensor_tensor(lam_t[:, 2, :], lam_t[:, 2, :], lam_t[:, 1, :], ALU.mult))
            link(v.tensor_tensor(lam_t[:, 2, :], lam_t[:, 2, :], lam_t[:, 0, :], ALU.mult))
            link(v.tensor_tensor(lam_t[:, 2, :], lam_t[:, 2, :], lam_t[:, 3, :], ALU.add))
            link(v.tensor_scalar(kdec[:, :], lam_t[:, 2, :], -0.5 * LRU_C, None, ALU.mult))
            dve.sem_inc(s_kd, 1)

            for j in range(JT):
                dve.wait_ge(s_in, JT + j + 1)
                dve.wait_ge(s_sg, j + 1)
                dve.wait_ge(s_zero, 1)
                v.tensor_tensor(vpad[:, j, :, LEFT_C:LEFT_C + CTX], ps[:, j, :].rearrange("p (s n) -> p s n", s=2),
                                sg[:, j, :].rearrange("p (s n) -> p s n", s=2), ALU.mult).then_inc(s_v, 1)

            def conv(tiles, src, dst, taps, wcol, bcol):
                for w in range(taps):
                    for j in tiles:
                        o = dst(j).rearrange("p (s n) -> p s n", s=2)
                        wc = par[:, wcol + JT * w + j:wcol + JT * w + j + 1]
                        if w == 0:
                            last = v.tensor_scalar(o, src[:, j, :, w:w + CTX], wc, par[:, bcol + j:bcol + j + 1],
                                                   ALU.mult, ALU.add)
                        else:
                            dve.wait_ge(s_dve, step[0] - len(tiles) + 1)
                            last = v.scalar_tensor_tensor(o, src[:, j, :, w:w + CTX], wc, o, ALU.mult, ALU.add)
                        mark(last)
                dve.wait_ge(s_dve, step[0])

            dve.wait_ge(s_v, 3)
            conv((0, 1, 2), vpad, lambda j: cat[:, JT + j, :], TAPS_C, C_DWW, C_DWB)
            dve.sem_inc(s_cvd, 1)
            for pair in ((0, 1), (2, 3)):
                dve.wait_ge(s_xa, pair[1] + 1)
                conv(pair, xpad, lambda j: u[:, j, :], TAPS_L, C_CONVW, C_CONVB)
                dve.sem_inc(s_u, 2)

            def one_minus_square(j):
                for d in range(2):
                    r, i, aa = (lru[j % 2][:, d, w, :] for w in range(3))
                    dve.wait_ge(s_co, 2 * j + d + 1)
                    v.scalar_tensor_tensor(i, i, 1.0, u[:, j, :], ALU.add, ALU.mult)
                    link(v.tensor_tensor(lru_sq, aa, aa, ALU.mult))
                    link(v.scalar_tensor_tensor(r, lru_sq, 1.0, r, ALU.add, ALU.mult))
                dve.sem_inc(s_sq1, 1)

            def scans(j):
                dve.wait_ge(s_ga, j + 1)
                for d in range(2):
                    r, i, aa = (lru[j % 2][:, d, w, :] for w in range(3))
                    dve.wait_ge(s_sqr, 2 * j + d + 1)
                    link(v.tensor_tensor(i, i, r, ALU.mult))
                    if d == 0:
                        link(v.tensor_tensor_scan(lru_hf, aa, i, 0.0, ALU.mult, ALU.add))
                    else:
                        link(v.tensor_tensor_scan(r[:, CTX - 1::-1], aa[:, CTX - 1::-1], i[:, CTX - 1::-1], 0.0,
                                                  ALU.mult, ALU.add))
                        link(v.tensor_tensor_scan(r[:, TOK - 1:CTX - 1:-1], aa[:, TOK - 1:CTX - 1:-1],
                                                  i[:, TOK - 1:CTX - 1:-1], r[:, 0:1], ALU.mult, ALU.add))
                        link(v.tensor_tensor(lru_hf, lru_hf, r, ALU.add))
                        link(v.tensor_tensor(cat[:, j, :], cat[:, j, :], lru_hf, ALU.mult))
                dve.sem_inc(s_lru, 1)

            for j in range(JT + 1):
                if j < JT:
                    one_minus_square(j)
                if j:
                    scans(j - 1)
            dve.wait_ge(s_col, 24)
            link(read_mods(0, 4, 12, 4))
            link(read_mods(1, 12, 24, 0))
            dve.sem_inc(s_mods, 1)
            for dst, l, i, pc0 in ((a2, 0, SC2, C_FFNG), (a1, 1, SC1, C_MIXG + 8), (a2, 1, SC2, C_FFNG + 8)):
                link(gain(dst, l, i, pc0))
                dve.sem_inc(s_a12, 1)
            dve.wait_ge(s_mean, 1)
            for j in range(JT):
                v.tensor_tensor(cat[:, JT + j, :], cat[:, JT + j, :], ps[:, 4, :], ALU.subtract).then_inc(s_xc, 1)
            invert(ln_r)
            dve.wait_ge(s_xc, JT)
            for j in range(JT):
                v.scalar_tensor_tensor(cat[:, JT + j, :], cat[:, JT + j, :], par[:, C_LNG + j:C_LNG + j + 1], ln_r,
                                       ALU.mult, ALU.mult).then_inc(s_nrm, 1)

            def add_residual(l, tiles, rows, bc_of):
                n_t = len(tiles)
                for c in range(2):
                    for i, t in enumerate(tiles):
                        m = c * n_t + i
                        g, n_bc = bc_of(t)
                        dve.wait_ge(s_bc, n_bc)
                        dve.wait_ge(s_op[l], m + 1)
                        tmp = junk[:, 512 * (m % 2):512 * (m % 2) + 512]
                        link(v.tensor_tensor(tmp, ps[:, m % 4, :], mb[g][:, 512 * c:512 * c + 512], ALU.mult))
                        v.tensor_tensor(x[:, t, 512 * c:512 * c + 512], x[:, t, 512 * c:512 * c + 512], tmp,
                                        ALU.add).then_inc(s_res[l], 1)

            dve.wait_ge(s_fill, 32)
            add_residual(0, range(NT), None, lambda t: ((0, 1) if cond_of(t) == CON else (1, 2)))

            def moe_norm(l, gain_of):
                tiles = toks(l)
                invert(rstd[:, 2 + l, tiles[0]:NT])
                for i, t in enumerate(tiles):
                    g, s, n_bc = gain_of(t)
                    dve.wait_ge(s_bc, n_bc)
                    link(v.scalar_tensor_tensor(hrow[:, t, :], x[:, t, :], rstd[:, 2 + l, t:t + 1], mb[g], ALU.mult, ALU.mult))
                    v.tensor_tensor(hrow[:, t, :], hrow[:, t, :], mb[s], ALU.add).then_inc(s_h[l], 1)

            def route(l):
                tiles = toks(l)
                n = len(tiles)
                w = E * n
                at = [1024]

                def tmp(size):
                    at[0] += size
                    assert RT + at[0] <= 12288
                    return rt(at[0] - size, size)

                def ranks(src, m):
                    before, equal, out = tmp(m * 16), tmp(m * 16), tmp(m * 4)
                    b4, e4 = (z.rearrange("p (m i j) -> p m i j", i=4, j=4) for z in (before, equal))
                    vj = src.unsqueeze(2).to_broadcast([P, m, 4, 4])
                    vi = src.unsqueeze(3).to_broadcast([P, m, 4, 4])
                    v.tensor_tensor(b4, vj, vi, ALU.is_gt)
                    link(v.tensor_tensor(e4, vj, vi, ALU.is_equal))
                    link(v.tensor_tensor(e4, e4, tie[:, :, :].unsqueeze(1).to_broadcast([P, m, 4, 4]), ALU.mult))
                    link(v.tensor_tensor(before, before, equal, ALU.add))
                    o = out.rearrange("p (m i) -> p m i", i=4)
                    link(v.tensor_reduce(o, b4, AX, ALU.add))
                    return o

                score, sel_, m1, gsum, wgt = tmp(w), tmp(w), tmp(w), tmp(4 * n), tmp(w)
                s3 = score.rearrange("p (t e) -> p t e", t=n)
                dve.wait_ge(s_sc[l], 1)
                v.tensor_copy(score, score_sb(l))
                link(v.tensor_tensor(sel_.rearrange("p (t e) -> p t e", t=n), score_sb(l).rearrange("p (t e) -> p t e", t=n),
                                     rbias[:, :].unsqueeze(1).to_broadcast([P, n, E]), ALU.add))
                r = ranks(sel_.rearrange("p (m i) -> p m i", i=4), 4 * n)
                link(v.tensor_scalar(m1, r.rearrange("p m i -> p (m i)"), 2.0, None, ALU.is_lt))
                link(v.tensor_tensor(wgt, sel_, m1, ALU.mult))
                link(v.tensor_reduce(gsum, wgt.rearrange("p (m i) -> p m i", i=4), AX, ALU.add))
                gr = ranks(gsum.rearrange("p (t g) -> p t g", t=n), n)
                link(v.tensor_scalar(gsum, gr.rearrange("p t g -> p (t g)"), 1.0, None, ALU.is_lt))
                mask = m1
                link(v.tensor_tensor(mask.rearrange("p (m i) -> p m i", i=4), m1.rearrange("p (m i) -> p m i", i=4),
                                     gsum.unsqueeze(2).to_broadcast([P, 4 * n, 4]), ALU.mult))
                v.tensor_copy(mask_b(l).rearrange("p t e -> p (t e)"), mask).then_inc(s_mask[l], 1)
                m3 = mask.rearrange("p (t e) -> p t e", t=n)
                w3 = wgt.rearrange("p (t e) -> p t e", t=n)
                wsum = tmp(n)
                link(v.tensor_tensor(wgt, score, mask, ALU.mult))
                link(v.tensor_reduce(wsum, w3, AX, ALU.add))
                link(v.reciprocal(wsum, wsum))
                link(v.tensor_tensor(w3, w3, wsum.unsqueeze(2).to_broadcast([P, n, E]), ALU.mult))
                dve.wait_ge(s_pos[l], 1)
                cmp_, ntile, incl, base = tmp(E * (MAXT - 1)), tmp(E), tmp(E), tmp(E)
                c3 = cmp_.rearrange("p (e m) -> p e m", e=E)
                link(v.tensor_tensor(c3, ps[:, 5, 0:E].unsqueeze(2).to_broadcast([P, E, MAXT - 1]),
                                     thr[:, :].unsqueeze(1).to_broadcast([P, E, MAXT - 1]), ALU.is_gt))
                link(v.tensor_reduce(ntile, c3, AX, ALU.add))
                link(v.tensor_scalar(ntile, ntile, 1.0, None, ALU.add))
                link(v.tensor_tensor_scan(incl, ones16[:, :], ntile, 0.0, ALU.mult, ALU.add))
                link(v.tensor_tensor(base, incl, ntile, ALU.subtract))
                v.tensor_copy(ctl[:, 0, :], ntile)
                v.tensor_copy(ctl[:, 1, :], base)
                v.tensor_copy(ctl[:, 2, :], incl)
                val, hl, eqs = tmp(w), tmp(2 * n), tmp(2 * w)
                val3 = val.rearrange("p (t e) -> p t e", t=n)
                hl3 = hl.rearrange("p (c t) -> p c t", c=2)
                link(v.tensor_scalar(base, base, float(MT), 1.0, ALU.mult, ALU.add))
                link(v.tensor_tensor(val3, ps[:, 4, 0:w].rearrange("p (t e) -> p t e", t=n),
                                     base.unsqueeze(1).to_broadcast([P, n, E]), ALU.add))
                link(v.tensor_tensor(val, val, mask, ALU.mult))
                link(v.tensor_reduce(hl3[:, 0, :], val3, AX, ALU.max))
                link(v.tensor_reduce(hl3[:, 1, :], val3, AX, ALU.add))
                link(v.tensor_tensor(hl3[:, 1, :], hl3[:, 1, :], hl3[:, 0, :], ALU.subtract))
                e4 = eqs.rearrange("p (c t e) -> p c t e", c=2, t=n)
                for c in range(2):
                    link(v.tensor_tensor(e4[:, c, :, :], val3, hl3[:, c, :].unsqueeze(2).to_broadcast([P, n, E]), ALU.is_equal))
                    link(v.tensor_tensor(e4[:, c, :, :], e4[:, c, :, :], w3, ALU.mult))
                    link(v.tensor_reduce(gates2[:, c, 0:n], e4[:, c, :, :], AX, ALU.add))
                link(v.tensor_scalar(hl, hl, -1.0, None, ALU.add))
                v.tensor_copy(row_i[:, :, 0:n], hl3)
                m = 2 * n
                d_, in_, s_ = tmp(m * GMAX), tmp(m * GMAX), tmp(m)
                d3, i3 = (z.rearrange("p (i g) -> p i g", i=m) for z in (d_, in_))
                link(v.tensor_tensor(d3, hl.unsqueeze(2).to_broadcast([P, m, GMAX]),
                                     iota_g[:, :].unsqueeze(1).to_broadcast([P, m, GMAX]), ALU.subtract))
                link(v.tensor_scalar(in_, d_, 0.0, None, ALU.is_ge))
                link(v.scalar_tensor_tensor(in_, d_, float(MT), in_, ALU.is_lt, ALU.mult))
                link(v.tensor_tensor(d_, d_, in_, ALU.mult))
                link(v.tensor_reduce(s_, d3, AX, ALU.add))
                v.tensor_scalar(oh_tile(l)[:, :, 0, :], i3, pcol[:, 1:2], None, ALU.mult)
                tn = tmp(m)
                link(v.tensor_copy(tn.rearrange("p (c t) -> p c t", c=2), tile_no[:, :, 0:n]))
                v.tensor_tensor(oh_tile(l)[:, :, 1, :], i3, tn.unsqueeze(2).to_broadcast([P, m, GMAX]), ALU.mult)
                link(v.tensor_tensor(oh_slot(l), s_.unsqueeze(2).to_broadcast([P, m, P]),
                                     iota_s[:, :].unsqueeze(1).to_broadcast([P, m, P]), ALU.is_equal))
                dve.sem_inc(s_oh[l], 1)
                dve.wait_ge(s_id[l], 1)
                ids = tmp(GMAX)
                link(v.tensor_scalar(ids, ps[:, 4, GMAX:2 * GMAX], 2.0 * P, pcol[:, 2:3], ALU.mult, ALU.add))
                link(v.tensor_tensor(gidx[:, :], ps[:, 4, 0:GMAX], ids, ALU.add))
                dve.sem_inc(s_rt[l], 1)

            def moe(l):
                total = dve.value_load(ctl[0:1, 2, E - 1:E], min_val=E, max_val=32)
                dve.sem_inc(s_y[l], 1)
                with dve.Fori(0, total) as g:
                    for c in range(2):
                        dve.wait_ge(s_sl[l], g * 2 + (c + 1))
                        v.tensor_tensor(act_in[:, P * c:P * c + P], act_sl[:, P * c:P * c + P], ps[:, UB[c], P * c:P * c + P],
                                        ALU.mult).then_inc(s_ac[l], 1)
                        dve.wait_ge(s_at[l], g * 2 + (c + 1))
                        v.tensor_copy(actT[:, c, :], ps[:, 3, P * c:P * c + P]).then_inc(s_aT[l], 1)
                    dve.wait_ge(s_dn[l], g + 1)
                    dve.wait_ge(s_yo[l], g * 32 + 16)
                    v.tensor_copy(y_sb, ps[:, 4, :]).then_inc(s_y[l], 1)

            def combine(l, gate_of):
                for i, t in enumerate(toks(l)):
                    g, n_bc = gate_of(t)
                    dve.wait_ge(s_yg[l][i], 32)
                    dve.wait_ge(s_bc, n_bc)
                    y0, y1 = yg[:, 0, i, :], yg[:, 1, i, :]
                    link(v.tensor_scalar(y0, y0, gates2[:, 0, i:i + 1], None, ALU.mult))
                    link(v.scalar_tensor_tensor(y0, y1, gates2[:, 1, i:i + 1], y0, ALU.mult, ALU.add))
                    link(v.tensor_tensor(y0, y0, mb[g], ALU.mult))
                    link(v.tensor_tensor(x[:, t, :], x[:, t, :], y0, ALU.add))
                    dve.sem_inc(s_x2[l], 1)

            moe_norm(0, lambda t: ((2, 3, 4) if cond_of(t) == CON else (0, 1, 6)))
            route(0)
            moe(0)
            combine(0, lambda t: ((0, 7) if cond_of(t) == CON else (1, 8)))

            normalise(1)
            modulate_columns(1)
            for t in range(NT):
                dve.wait_ge(s_qkv, t + 1)
                v.tensor_copy(kv[:, t, :], ps[:, t, :]).then_inc(s_qkve, 1)
            for c in range(2):
                for i in range(2):
                    dve.wait_ge(s_qkv, NT + 2 * c + i + 1)
                    v.tensor_copy(q[:, i, 512 * c:512 * c + 512], ps[:, 4 + 2 * c + i, :]).then_inc(s_qkve, 1)
            dve.wait_ge(s_qkve, 8)

            def head_norm(view, squares, off, heads, tiles, gains, n_sq):
                dve.wait_ge(s_sq, n_sq)
                m = heads * tiles
                st = qk_ss[:, 0, off:off + m]
                link(v.tensor_reduce(st, squares.rearrange("p (m n) -> p m n", m=m), AX, ALU.add))
                dve.sem_inc(s_qss, 1)
                invert(st)
                for t in range(tiles):
                    z = view(t)
                    link(v.tensor_tensor(z, z, st[:, heads * t:heads * t + heads].unsqueeze(2).to_broadcast([P, heads, DH]),
                                         ALU.mult))
                    mark(v.tensor_tensor(z, z, gains[:, :].unsqueeze(1).to_broadcast([P, heads, DH]), ALU.mult))
                dve.wait_ge(s_dve, step[0])

            def rope(flat, heads, i):
                z = flat.rearrange("p (h a f n) -> p h a f n", h=heads, a=2, f=2)
                m = heads * 64
                t0, t1, t2, t3 = (rope_t[:, w, 0:m].rearrange("p (h a n) -> p h a n", h=heads, a=2) for w in range(4))
                cos, sin = (trig[:, i, w, :, :].unsqueeze(1).to_broadcast([P, heads, 2, 32]) for w in range(2))
                x1, x2 = z[:, :, :, 0, :], z[:, :, :, 1, :]
                v.tensor_tensor(t0, x1, cos, ALU.mult)
                v.tensor_tensor(t1, x2, sin, ALU.mult)
                v.tensor_tensor(t2, x2, cos, ALU.mult)
                link(v.tensor_tensor(t3, x1, sin, ALU.mult))
                link(v.tensor_tensor(x1, t0, t1, ALU.subtract))
                link(v.tensor_tensor(x2, t2, t3, ALU.add))

            head_norm(lambda t: kv[:, t, 0:KVH * DH].rearrange("p (h n) -> p h n", h=KVH), sq_big[:, 0:1024], 0, KVH, NT, kg, 1)
            for i in range(2):
                rope(kv[:, CT + i, 0:KVH * DH], KVH, i)
            dve.sem_inc(s_qn, 1)
            head_norm(lambda t: q[:, t, :].rearrange("p (h n) -> p h n", h=HEADS), sq_big[:, 1024:3072], 8, HEADS, 2, qg, 2)
            for i in range(2):
                rope(q[:, i, :], HEADS, i)
            dve.sem_inc(s_qn, 1)
            for g in range(6):
                dve.wait_ge(s_qkT, g + 1)
                if g < 2:
                    v.tensor_copy(kT[:, g, :], ps[:, g, :]).then_inc(s_qkTe, 1)
                else:
                    h = 2 * (g - 2)
                    v.tensor_copy(qT[:, h:h + 2, :], ps[:, g, :].rearrange("p (h n) -> p h n", h=2)).then_inc(s_qkTe, 1)
            scale = float(DH) ** -0.5

            def score_max(n):
                dve.wait_ge(s_s, n + 1)
                link(v.tensor_reduce(att[:, 0, n:n + 1], ps[:, n % 2, :], AX, ALU.max))
                v.tensor_scalar(att[:, 0, n:n + 1], att[:, 0, n:n + 1], -scale, None, ALU.mult).then_inc(s_m, 1)

            score_max(0)
            for n in range(2 * HEADS):
                if n + 1 < 2 * HEADS:
                    score_max(n + 1)
                dve.wait_ge(s_p, n + 1)
                link(v.reciprocal(att[:, 2, n:n + 1], att[:, 1, n:n + 1]))
                v.tensor_scalar(prob[:, n % 2, :], prob[:, n % 2, :], att[:, 2, n:n + 1], None, ALU.mult).then_inc(s_pn, 1)
                if n % 2 == 1 and n >= 3:
                    h = n // 2 - 1
                    dve.wait_ge(s_o, h + 1)
                    v.tensor_copy(oT[:, h, :], ps[:, 4 + h % 2, 0:SEQ]).then_inc(s_oe, 1)
            dve.wait_ge(s_o, HEADS)
            v.tensor_copy(oT[:, HEADS - 1, :], ps[:, 4 + (HEADS - 1) % 2, 0:SEQ]).then_inc(s_oe, 1)
            add_residual(1, range(CT, NT), None, lambda t: (0, 9))
            moe_norm(1, lambda t: (2, 3, 11))
            route(1)
            moe(1)
            combine(1, lambda t: (0, 12))
            invert(rstd[:, 1, 0:2])
            dve.wait_ge(s_fg, 16)
            for i, t in enumerate(range(CT, NT)):
                v.scalar_tensor_tensor(fin[:, i, :], x[:, t, :], rstd[:, 1, i:i + 1], fing, ALU.mult,
                                       ALU.mult).then_inc(s_fin, 1)

        def prob_columns(act, s, n):
            h, t = n // 2, n % 2
            act.wait_ge(s_pt, n + 1)
            if h >= 2:
                act.wait_ge(s_o, h - 1)
            s.activation(pT[:, h % 2, :, P * t:P * t + P], ps[:, 2 + n % 2, :].rearrange("p (k n) -> p k n", k=NT),
                         ACT.Copy).then_inc(s_pte, 1)

        @block.scalar
        def _(act):
            s = nc.scalar
            act.dma_start(x[:, 0:CT, :], a["ctx"].rearrange("b (t p) d -> p (b t) d", p=P)).then_inc(s_x, 16)
            act.dma_start(x[:, CT:NT, :], a["x"].rearrange("b (t p) d -> p (b t) d", p=P)).then_inc(s_x, 16)
            act.wait_ge(s_pc, 1)
            act.wait_ge(s_const, 1)
            s.activation(cond[:, :, 0:2], par[:, 0:16].rearrange("p (v k) -> p k v", v=2), ACT.Silu).then_inc(s_cond, 1)

            def squares(row, which, tiles, after=None):
                for i, t in enumerate(tiles):
                    if after:
                        after(i)
                    if i:
                        act.wait_ge(s_ss[which], i)
                    at = i if which == 4 else t
                    s.activation(junk, x[:, t, :], ACT.Square, accum_out=ss[:, row, at:at + 1]).then_inc(s_ss[which], 1)

            def rms(out, src, n, which=None, count=0):
                if which is not None:
                    act.wait_ge(s_ss[which], count)
                s.activation(out, src, ACT.Sqrt, scale=1.0 / n, bias=epsc[:, 0:1]).then_inc(s_rms, 1)

            act.wait_ge(s_x, 32)
            squares(0, 0, range(NT))
            rms(rstd[:, 0, :], ss[:, 0, :], D, 0, NT)

            ada = [0]

            def ada_read():
                n = ada[0]
                i = ADA_AT[n]
                act.wait_ge(used[i % RING], i // RING + 1)
                if n >= 2:
                    act.wait_ge(s_col, n - 1)
                s.activation(ada_part[:, n % 2, :], ps[:, 6, :], ACT.Copy).then_inc(s_part, 1)
                ada[0] += 1

            for n in range(4):
                ada_read()

            def modulate_columns(l):
                for k in range(1, KD, 2):
                    act.wait_ge(s_xT[l], k + 1)
                    for vv, lo in ((CON, 0), (LAT, CTX)):
                        last = s.activation(hT[:, k, lo:lo + 256], ps[:, k % 4, lo:lo + 256], ACT.Identity,
                                            scale=a1[:, l, k, vv:vv + 1], bias=mods[:, l, 8 * SH1 + k, vv:vv + 1])
                    last.then_inc(s_hTa[l], 1)

            act.wait_ge(s_mods, 1)
            modulate_columns(0)
            act.wait_ge(s_kd, 1)
            s.activation(lam_t[:, 0, :], lam_t[:, 0, :], ACT.Exp, scale=-1.0).then_inc(s_act, 1)
            act.wait_ge(s_kd, 2)
            s.activation(lam_t[:, 2, :], lam_t[:, 1, :], ACT.Ln).then_inc(s_act, 1)
            for m in range(4 * JT):
                part, j = m // JT, m % JT
                act.wait_ge(s_in, m + 1)
                if part == 0:
                    s.activation(sg[:, j, :], ps[:, j, :], ACT.Sigmoid).then_inc(s_sg, 1)
                elif part == 2:
                    act.wait_ge(s_zero, 1)
                    s.activation(xpad[:, j, :, LEFT_L:LEFT_L + CTX], ps[:, j, :].rearrange("p (s n) -> p s n", s=2),
                                 ACT.Copy).then_inc(s_xa, 1)
                elif part == 3:
                    s.activation(cat[:, j, :], ps[:, j, :], ACT.Gelu_apprx_tanh).then_inc(s_ga, 1)
                ada_read()
            act.wait_ge(s_kd, 3)
            def coefficients(j):
                if j >= 2:
                    act.wait_ge(s_lru, j - 1)
                for d in range(2):
                    r, i, aa = (lru[j % 2][:, d, w, :] for w in range(3))
                    qd, col = 2 * j + d, 4 * d + j
                    act.wait_ge(s_gm, qd + 1)
                    s.activation(r, ps[:, 4, :], ACT.Tanh, scale=0.5, bias=hb[:, 0, col:col + 1]).then_inc(s_act, 1)
                    s.activation(i, ps[:, 5, :], ACT.Tanh, scale=0.5, bias=hb[:, 1, col:col + 1]).then_inc(s_gr, 1)
                    act.wait_ge(s_act, 2 + 2 * qd + 1)
                    kd = kdec[:, col:col + 1]
                    s.activation(aa, r, ACT.Exp, scale=kd, bias=kd).then_inc(s_act, 1)
                    act.wait_ge(s_act, 2 + 2 * qd + 2)
                    s.activation(r, r, ACT.Tanh, scale=kd, bias=kd).then_inc(s_co, 1)

            def roots(j):
                act.wait_ge(s_sq1, j + 1)
                for d in range(2):
                    r = lru[j % 2][:, d, 0, :]
                    s.activation(r, r, ACT.Sqrt, scale=-0.25).then_inc(s_sqr, 1)

            for j in range(JT + 1):
                if j < JT:
                    coefficients(j)
                if j:
                    roots(j - 1)
            for _ in range(4):
                ada_read()
            for j in range(JT):
                act.wait_ge(s_xc, j + 1)
                s.activation(hT[:, j, :], cat[:, JT + j, :], ACT.Square).then_inc(s_sqc, 1)
            act.wait_ge(s_var, 1)
            rms(ln_r, ps[:, 5, :], 1.0)
            for j in range(JT):
                act.wait_ge(s_nrm, j + 1)
                s.activation(cat[:, JT + j, :], cat[:, JT + j, :], ACT.Silu,
                             bias=par[:, C_LNB + j:C_LNB + j + 1]).then_inc(s_cat, 1)

            def read_broadcast(n, *free):
                for sm, val in free:
                    act.wait_ge(sm, val)
                act.wait_ge(s_bcm, n + 1)
                s.activation(mb[BC[n][4]].rearrange("p (b n) -> p b n", b=2), ps[:, 6:8, :], ACT.Copy).then_inc(s_bc, 1)

            read_broadcast(0, (s_lru, JT))
            read_broadcast(1)
            read_broadcast(2, (s_cvd, 1), (s_cvp, 1))
            read_broadcast(3)

            def after_residual(l, n_t):
                return lambda i: act.wait_ge(s_res[l], n_t + i + 1)

            act.wait_ge(s_res[0], 2 * NT)
            squares(2, 1, range(NT))
            rms(rstd[:, 2, :], ss[:, 2, :], D, 1, NT)
            read_broadcast(4)
            read_broadcast(5)

            def router(l):
                tiles = toks(l)
                n = len(tiles)
                for i, t in enumerate(tiles):
                    act.wait_ge(s_h2m[l], i + 1)
                    s.activation(hT[:, :, P * t:P * t + P].rearrange("p (b k) n -> p b k n", b=2),
                                 ps[:, 2 * (i % 2):2 * (i % 2) + 2, :].rearrange("p b (k n) -> p b k n", k=4),
                                 ACT.Copy).then_inc(s_h2[l], 1)
                act.wait_ge(s_rp[l], 1)
                s.activation(ada_part[:, 0, 0:P * n], ps[:, 4, 0:P * n], ACT.Copy).then_inc(s_rpe[l], 1)
                act.wait_ge(s_lg[l], 1)
                s.activation(score_sb(l), ps[:, 5, 0:E * n], ACT.Sigmoid).then_inc(s_sc[l], 1)

            def moe(l):
                act.wait_ge(s_rt[l], 1)
                total = act.value_load(ctl[0:1, 2, E - 1:E], min_val=E, max_val=32)

                def tile_columns(count):
                    act.wait_ge(s_xt[l], count + 1)
                    s.activation(xgT.rearrange("p k n -> p (k n)"), ps[:, 0, :], ACT.Copy).then_inc(s_xgT[l], 1)

                act.sem_inc(s_yo[l], 16)
                tile_columns(1)
                with act.Fori(0, total) as g:
                    for c in range(2):
                        act.wait_ge(s_gu[l], g * 2 + (c + 1))
                        s.activation(act_sl[:, P * c:P * c + P], ps[:, GB[c], P * c:P * c + P], ACT.Silu).then_inc(s_sl[l], 1)
                    tile_columns(g + 2)
                    act.wait_ge(s_y[l], g + 2)
                    rows = y_dram.rearrange("(g s) (h n) -> g h s n", s=MT, h=2)
                    for hf in range(2):
                        act.dma_start(rows[g, hf], y_sb[64 * hf:64 * hf + 64, :]).then_inc(s_yo[l], 16)
                act.wait_ge(s_yo[l], total * 32 + 16)
                act.sem_inc(s_yall[l], 1)

            router(0)
            moe(0)
            read_broadcast(6, (s_h[0], NT))
            read_broadcast(7)
            squares(1, 2, range(NT), lambda i: act.wait_ge(s_x2[0], i + 1))
            rms(rstd[:, 1, :], ss[:, 1, :], D, 2, NT)
            modulate_columns(1)
            act.wait_ge(s_qkve, NT)
            s.activation(sq_big[:, 0:1024].rearrange("p (t n) -> p t n", t=NT), kv[:, :, 0:KVH * DH], ACT.Square).then_inc(s_sq, 1)
            act.wait_ge(s_qkve, 8)
            s.activation(sq_big[:, 1024:3072].rearrange("p (t n) -> p t n", t=2), q, ACT.Square).then_inc(s_sq, 1)
            act.wait_ge(s_qss, 1)
            rms(qk_ss[:, 0, 0:8], qk_ss[:, 0, 0:8], DH)
            act.wait_ge(s_qss, 2)
            rms(qk_ss[:, 0, 8:24], qk_ss[:, 0, 8:24], DH)
            scale = float(DH) ** -0.5
            for n in range(2 * HEADS):
                act.wait_ge(s_m, n + 1)
                if n >= 2:
                    act.wait_ge(s_pt, n - 1)
                s.activation(prob[:, n % 2, :], ps[:, n % 2, :], ACT.Exp, scale=scale, bias=att[:, 0, n:n + 1],
                             accum_out=att[:, 1, n:n + 1]).then_inc(s_p, 1)
                if n >= 1:
                    prob_columns(act, s, n - 1)
            prob_columns(act, s, 2 * HEADS - 1)
            read_broadcast(8, (s_qn, 2))
            act.wait_ge(s_res[1], 4)
            squares(3, 3, range(CT, NT))
            rms(rstd[:, 3, CT:NT], ss[:, 3, CT:NT], D, 3, 2)
            read_broadcast(9)
            read_broadcast(10)
            router(1)
            moe(1)
            read_broadcast(11, (s_h[1], 2))
            squares(1, 4, range(CT, NT), lambda i: act.wait_ge(s_x2[1], i + 1))
            rms(rstd[:, 1, 0:2], ss[:, 1, 0:2], D, 4, 2)

        @block.gpsimd
        def _(pool):
            g = nc.gpsimd
            step = [0]

            def link(ins):
                step[0] += 1
                ins.then_inc(s_pool, 1)
                pool.wait_ge(s_pool, step[0])

            link(g.memset(ident[:, :], 0.0))
            link(g.affine_select(ident[:, :], ident[:, :], [[-1, P]], ALU.not_equal, 1.0, base=0, channel_multiplier=1))
            link(g.memset(sel[:, :], 0.0))
            for j in range(4):
                link(g.affine_select(sel[:, :], sel[:, :], [[-1, E]], ALU.not_equal, 1.0, base=-32 * j, channel_multiplier=1))
            link(g.memset(epsc[:, :], EPS))
            link(g.memset(cond[:, :, :], 0.0))
            pool.sem_inc(s_const, 1)
            for kind, name in ((0, "lru_w_r"), (1, "lru_w_i")):
                for d in range(2):
                    for hf in range(2):
                        src = a[name][0, d].rearrange("(j h) i o -> h i j o", h=2)[hf]
                        g.dma_start(wbd[64 * hf:64 * hf + 64, kind, d, :, :], src).then_inc(s_aux, 16)
            link(g.memset(rw[:, :, :], 0.0))
            g.dma_start(rw[:, :, 0:E], a["router_w"].rearrange("(k p) e -> p k e", p=P)).then_inc(s_aux, 16)
            g.dma_start(rbias[:, :], a["router_bias"].unsqueeze(0).to_broadcast([P, E])).then_inc(s_aux, 16)
            g.dma_start(qg[:, :], a["at_q_norm_g"].to_broadcast([P, DH])).then_inc(s_aux, 16)
            g.dma_start(kg[:, :], a["at_k_norm_g"].to_broadcast([P, DH])).then_inc(s_aux, 16)
            g.dma_start(trig[:, :, :, :, :].rearrange("p t w a n -> p t (w a n)"),
                        a["rope"].rearrange("(t p) n -> p t n", p=P)).then_inc(s_aux, 16)
            link(g.memset(vpad[:, :, :, 0:LEFT_C], 0.0))
            link(g.memset(vpad[:, :, :, LEFT_C + CTX:VP], 0.0))
            link(g.memset(xpad[:, :, :, 0:LEFT_L], 0.0))
            link(g.memset(xpad[:, :, :, LEFT_L + CTX:XP], 0.0))
            link(g.memset(ones512[:, :], 1.0 / DL))
            link(g.memset(onesb[:, :], 1.0))
            link(g.memset(ones16[:, :], 1.0))
            link(g.memset(trib[:, :], 1.0))
            link(g.affine_select(trib[:, :], trib[:, :], [[1, P]], ALU.is_ge, 0.0, base=-1, channel_multiplier=-1))
            kw = dict(allow_small_or_imprecise_dtypes=True)
            link(g.iota(iota_s[:, :], [[0, 2], [1, MT]], base=0, channel_multiplier=0, **kw))
            link(g.iota(iota_g[:, :], [[MT, GMAX]], base=0, channel_multiplier=0, **kw))
            link(g.iota(thr[:, :], [[MT, MAXT - 1]], base=MT, channel_multiplier=0, **kw))
            link(g.iota(tile_no[:, :, :], [[0, 2], [1, NT]], base=0, channel_multiplier=0, **kw))
            link(g.iota(pcol[:, 0:1], [[0, 1]], base=0, channel_multiplier=1, **kw))
            link(g.iota(tie[:, :, :], [[1, 4], [-1, 4]], base=0, channel_multiplier=0, **kw))
            link(g.tensor_scalar(tie[:, :, :], tie[:, :, :], 0.0, None, ALU.is_gt))
            link(g.tensor_scalar(pcol[:, 1:2], pcol[:, 0:1], 2.0, None, ALU.mult))
            link(g.tensor_scalar(pcol[:, 2:3], pcol[:, 0:1], 64.0, None, ALU.is_ge))
            pool.sem_inc(s_zero, 1)

            pool.wait_ge(s_pc, 1)
            pool.wait_ge(s_v, JT)
            for i in range(2):
                g.dma_start(y_dram[E * MT + TOK * i:E * MT + TOK * i + TOK, :].rearrange("(t p) d -> p t d", p=P),
                            x[:, :, :]).then_inc(s_fill, 16)
            j = JT - 1
            o = cat[:, JT + j, :].rearrange("p (s n) -> p s n", s=2)
            tap = conv_tap.rearrange("p (s n) -> p s n", s=2)
            for w in range(TAPS_C):
                wc = par[:, C_DWW + JT * w + j:C_DWW + JT * w + j + 1]
                if w == 0:
                    link(g.tensor_scalar(o, vpad[:, j, :, 0:CTX], wc, par[:, C_DWB + j:C_DWB + j + 1], ALU.mult, ALU.add))
                else:
                    link(g.tensor_scalar(tap, vpad[:, j, :, w:w + CTX], wc, None, ALU.mult))
                    link(g.tensor_tensor(o, o, tap, ALU.add))
            pool.sem_inc(s_cvp, 1)

            def moe(l):
                tiles = toks(l)
                n = len(tiles)
                for i, t in enumerate(tiles):
                    pool.wait_ge(s_h[l], i + 1)
                    g.dma_start(h_dram[l][P * i:P * i + P, :], hrow[:, t, :]).then_inc(s_hst[l], 16)
                pool.wait_ge(s_rt[l], 1)
                pool.wait_ge(s_hst[l], 16 * n)
                total = pool.value_load(ctl[0:1, 2, E - 1:E], min_val=E, max_val=32)
                halves = h_dram[l].rearrange("t (h n) -> (t h) n", h=2)
                with pool.Fori(0, total + 1) as k:
                    pool.wait_ge(s_xt[l], k + 1)
                    g.tensor_copy(gcur[:, :], gidx[:, bass.ds(k, 1)]).then_inc(s_gc[l], 1)
                    pool.wait_ge(s_gc[l], k + 1)
                    pool.sem_inc(s_gcd, 1)
                    g.indirect_dma_start(xg, None, halves, bass.IndirectOffsetOnAxis(gcur[:, 0:1], 0)).then_inc(s_xg[l], 16)
                pool.wait_ge(s_yall[l], 1)
                for i in range(n):
                    for c in range(2):
                        g.indirect_dma_start(yg[:, c, i, :], None, y_dram,
                                             bass.IndirectOffsetOnAxis(row_i[:, c, i:i + 1], 0)).then_inc(s_yg[l][i], 16)

            moe(0)
            moe(1)
            g.dma_start(fing, a["final_norm_g"].unsqueeze(0).to_broadcast([P, D])).then_inc(s_fg, 16)


AUX = 8 + 5
GB, UB = (1, 5), (2, 6)
ADA_AT = [i for i, (kind, _, _) in enumerate(PRE) if kind == "ada"]

INS = ["x", "c", "ctx", "c_ctx", "ada_w", "ada_b", "norm_mix_g", "norm_ffn_g", "ev_w_in", "ev_w_out",
       "lru_conv_w", "lru_conv_b", "lru_w_r", "lru_b_r", "lru_w_i", "lru_b_i", "lru_lambda",
       "cf_dw_w", "cf_dw_b", "cf_ln_g", "cf_ln_b", "at_w_qkv", "at_w_out", "at_q_norm_g", "at_k_norm_g",
       "router_w", "router_bias", "exp_w_gate", "exp_w_up", "exp_w_down", "final_norm_g"]


def rope_table():
    grid_w, half = 64, 64
    freq = (np.float32(10000.0) ** (-np.arange(0, half, 2, dtype=np.float32) / np.float32(half))).astype(np.float32)
    t = np.arange(SEQ)
    ang = np.stack([(t // grid_w).astype(np.float32)[:, None] * freq, (t % grid_w).astype(np.float32)[:, None] * freq], 1)
    return np.stack([np.cos(ang), np.sin(ang)], 1).reshape(SEQ, 128).astype(np.float32)


def kernel(**inputs):
    import concourse.bacc as bacc
    from concourse.bass_utils import run_bass_kernel_spmd

    nc = bacc.Bacc("TRN2", target_bir_lowering=False, num_devices=1)
    arrays, aps = {}, {}
    for name in INS:
        v = np.ascontiguousarray(inputs[name])
        arrays[f"in_{name}"] = v
        aps[name] = nc.dram_tensor(f"in_{name}", v.shape, mybir.dt.from_np(v.dtype), kind="ExternalInput").ap()
    table = rope_table()
    arrays["in_rope"] = table
    aps["rope"] = nc.dram_tensor("in_rope", table.shape, F32, kind="ExternalInput").ap()
    aps["out"] = nc.dram_tensor("out_0", (1, SEQ, D), F32, kind="ExternalOutput").ap()
    build(nc, aps)
    r = run_bass_kernel_spmd(nc, [arrays], core_ids=[0])
    return r.results[0]["out_0"]
```
